# Optimizing a Trainium2 kernel written in Bass

```python
import jax, jax.numpy as jnp
from jax import lax
import numpy as np

D_MODEL = 1024
BATCH = 1
SEQ = 1024
DEPTH = 1
DEC_BATCH = 1
DEC_SEQ = 64
PAST_LEN = 2048

CHUNK = 64
N_META = 16
EPS = 1e-6
D_POOL = D_MODEL // 2
POOL_WINDOWS = (2, 4, 8, 16)
N_POOL_GROUPS = len(POOL_WINDOWS)
POOL_GROUP_DIM = D_POOL // N_POOL_GROUPS
POOL_PAD = max(POOL_WINDOWS) - 1
GLA_HEADS = 4
GLA_DK = D_MODEL // 16
GLA_DV = D_MODEL // 8
D_QK = GLA_HEADS * GLA_DK
D_V = GLA_HEADS * GLA_DV
GATE_RANK = 16
GATE_TAU = 16.0
D_MIX = D_POOL + D_V
IN_SPLITS = (D_POOL, D_POOL + D_QK, D_POOL + 2 * D_QK, D_POOL + 2 * D_QK + D_V, D_POOL + 2 * D_QK + 2 * D_V)
D_IN = D_POOL + 2 * D_QK + 2 * D_V + GATE_RANK
N_GROUPS = 4
EXPERTS_PER_GROUP = 8
N_EXPERTS = N_GROUPS * EXPERTS_PER_GROUP
D_EXPERT = D_MODEL // 2
MOE_BLOCK = 128

kernel_name = 'hybrid_pool_gla_hiermoe_stream_step'

def rmsnorm(x, g):
    xf = x.astype(jnp.float32)
    y = xf * lax.rsqrt(jnp.mean(xf * xf, axis=-1, keepdims=True) + EPS)
    return y * g.astype(jnp.float32)

def pool_mix(u, prefix, n_valid_prefix, w_pool, pool_scale):
    B, L, _ = u.shape
    ext = jnp.concatenate([prefix.astype(u.dtype), u], axis=1)
    cs = jnp.cumsum(ext.astype(jnp.float32), axis=1)
    cs = jnp.pad(cs, ((0, 0), (1, 0), (0, 0)))
    t = jnp.arange(L)
    outs = []
    for g, w in enumerate(POOL_WINDOWS):
        sl = slice(g * POOL_GROUP_DIM, (g + 1) * POOL_GROUP_DIM)
        s = cs[:, POOL_PAD + 1:POOL_PAD + 1 + L, sl] - cs[:, POOL_PAD + 1 - w:POOL_PAD + 1 - w + L, sl]
        cnt = jnp.minimum(t + n_valid_prefix + 1, w).astype(jnp.float32)
        outs.append(s / cnt[None, :, None])
    pooled = jnp.concatenate(outs, axis=-1) - u.astype(jnp.float32)
    pooled = pooled.reshape(B, L, N_POOL_GROUPS, POOL_GROUP_DIM)
    y = jnp.einsum('blgc,gcd->blgd', pooled, w_pool.astype(jnp.float32)).reshape(B, L, D_POOL)
    return y * pool_scale.astype(jnp.float32), ext[:, -POOL_PAD:]

def gla_chunked(q, k, v, log_a, s0, chunk):
    B, L, H, DK = q.shape
    DV = v.shape[-1]
    N = L // chunk
    q = q.reshape(B, N, chunk, H, DK)
    k = k.reshape(B, N, chunk, H, DK)
    v = v.reshape(B, N, chunk, H, DV)
    b = jnp.cumsum(log_a.reshape(B, N, chunk, H, DK), axis=2)
    b_last = b[:, :, -1]
    q_i = q * jnp.exp(b)
    k_i = k * jnp.exp(-b)
    scores = jnp.einsum('bnchk,bnshk->bnhcs', q_i, k_i)
    mask = jnp.tril(jnp.ones((chunk, chunk), dtype=bool))
    scores = jnp.where(mask, scores, 0.0)
    o_intra = jnp.einsum('bnhcs,bnshv->bnchv', scores, v)
    k_dec = k * jnp.exp(b_last[:, :, None] - b)
    kv = jnp.einsum('bnchk,bnchv->bnhkv', k_dec, v)
    decay = jnp.exp(b_last)

    def step(S, inp):
        dec, kvn = inp
        return dec[..., None] * S + kvn, S

    s_fin, s_in = lax.scan(step, s0, (jnp.moveaxis(decay, 1, 0), jnp.moveaxis(kv, 1, 0)))
    s_in = jnp.moveaxis(s_in, 0, 1)
    o_inter = jnp.einsum('bnchk,bnhkv->bnchv', q_i, s_in)
    return (o_intra + o_inter).reshape(B, L, H, DV), s_fin

def token_mixer(xn, pool_prefix, n_valid_prefix, s0, chunk, lead_pad,
                w_in, w_gate_up, b_gate, w_pool, pool_scale, gla_norm, w_out):
    B, L, _ = xn.shape
    f32 = jnp.float32
    proj = xn @ w_in
    u, q, k, v, r, z = jnp.split(proj, IN_SPLITS, axis=-1)
    pool_y, pool_state = pool_mix(u, pool_prefix, n_valid_prefix, w_pool, pool_scale)
    log_a = jax.nn.log_sigmoid(z.astype(f32) @ w_gate_up.astype(f32) + b_gate.astype(f32)) / GATE_TAU
    qh = q.astype(f32).reshape(B, L, GLA_HEADS, GLA_DK) * (GLA_DK ** -0.5)
    kh = k.astype(f32).reshape(B, L, GLA_HEADS, GLA_DK)
    vh = v.astype(f32).reshape(B, L, GLA_HEADS, GLA_DV)
    ah = log_a.reshape(B, L, GLA_HEADS, GLA_DK)
    if lead_pad:
        padw = ((0, 0), (lead_pad, 0), (0, 0), (0, 0))
        qh, kh, vh, ah = jnp.pad(qh, padw), jnp.pad(kh, padw), jnp.pad(vh, padw), jnp.pad(ah, padw)
    o, s_new = gla_chunked(qh, kh, vh, ah, s0.astype(f32), chunk)
    o = o[:, lead_pad:]
    o = o * lax.rsqrt(jnp.mean(o * o, axis=-1, keepdims=True) + EPS) * gla_norm.astype(f32).reshape(GLA_HEADS, GLA_DV)
    o = o.reshape(B, L, D_V) * jax.nn.silu(r.astype(f32))
    mix = jnp.concatenate([pool_y, o], axis=-1).astype(xn.dtype) @ w_out
    return mix, pool_state, s_new

def hier_moe(x, w_rg, b_rg, w_re, b_re, w_eg, w_eu, w_ed):
    T, D = x.shape
    xf = x.astype(jnp.float32)
    p_group = jax.nn.softmax(xf @ w_rg.astype(jnp.float32) + b_rg.astype(jnp.float32), axis=-1)
    g = jnp.argmax(p_group, axis=-1)
    p_g = jnp.max(p_group, axis=-1, keepdims=True)
    le = (xf @ w_re.astype(jnp.float32) + b_re.astype(jnp.float32)).reshape(T, N_GROUPS, EXPERTS_PER_GROUP)
    le_sel = jnp.einsum('tge,tg->te', le, jax.nn.one_hot(g, N_GROUPS, dtype=jnp.float32))
    top_v, top_i = lax.top_k(jax.nn.softmax(le_sel, axis=-1), 2)
    gates = p_g * top_v / jnp.sum(top_v, axis=-1, keepdims=True)
    expert = g[:, None].astype(jnp.int32) * EXPERTS_PER_GROUP + top_i.astype(jnp.int32)
    A = 2 * T
    flat_e = expert.reshape(-1)
    flat_gate = gates.reshape(-1)
    order = jnp.argsort(flat_e)
    sorted_e = flat_e[order]
    counts = jnp.bincount(flat_e, length=N_EXPERTS)
    padded = (counts + MOE_BLOCK - 1) // MOE_BLOCK * MOE_BLOCK
    start = jnp.cumsum(counts) - counts
    ends = jnp.cumsum(padded)
    pstart = ends - padded
    dest = pstart[sorted_e] + jnp.arange(A) - start[sorted_e]
    R = (A + N_EXPERTS * (MOE_BLOCK - 1) + MOE_BLOCK - 1) // MOE_BLOCK * MOE_BLOCK
    NB = R // MOE_BLOCK
    slot_tok = jnp.full((R,), T, jnp.int32).at[dest].set((order // 2).astype(jnp.int32))
    slot_gate = jnp.zeros((R,), jnp.float32).at[dest].set(flat_gate[order])
    block_e = jnp.clip(jnp.searchsorted(ends, jnp.arange(NB) * MOE_BLOCK, side='right'), 0, N_EXPERTS - 1)
    x_pad = jnp.concatenate([x, jnp.zeros((1, D), x.dtype)], axis=0)
    xs = x_pad[slot_tok].reshape(NB, MOE_BLOCK, D)

    def expert_block(args):
        xb, e = args
        h = jax.nn.silu(xb @ w_eg[e]) * (xb @ w_eu[e])
        return h @ w_ed[e]

    ys = lax.map(expert_block, (xs, block_e)).reshape(R, D)
    ys = ys.astype(jnp.float32) * slot_gate[:, None]
    out = jax.ops.segment_sum(ys, slot_tok, num_segments=T + 1)[:T]
    return out.astype(x.dtype)

def encoder_layer(x, pool_prefix, n_valid_prefix, s0, chunk, lead_pad,
                  norm_mix, w_in, w_gate_up, b_gate, w_pool, pool_scale, gla_norm, w_out,
                  norm_ffn, w_rg, b_rg, w_re, b_re, w_eg, w_eu, w_ed):
    B, L, D = x.shape
    xn = rmsnorm(x, norm_mix).astype(x.dtype)
    mix, pool_state, s_new = token_mixer(xn, pool_prefix, n_valid_prefix, s0, chunk, lead_pad,
                                         w_in, w_gate_up, b_gate, w_pool, pool_scale, gla_norm, w_out)
    h = x + mix.astype(x.dtype)
    hn = rmsnorm(h, norm_ffn).astype(x.dtype).reshape(B * L, D)
    h = h + hier_moe(hn, w_rg, b_rg, w_re, b_re, w_eg, w_eu, w_ed).reshape(B, L, D)
    return h, pool_state, s_new

def setup_inputs(seed: int = 0) -> dict:
    key = jax.random.key(seed)
    ks = jax.random.split(key, 24)
    n = lambda i, shape: jax.random.normal(ks[i], shape, jnp.float32)
    return {
        'x_prompt': n(0, (BATCH, SEQ, D_MODEL)),
        'x_sample': n(1, (DEC_BATCH, DEC_SEQ, D_MODEL)),
        'state_pool': n(2, (DEPTH, DEC_BATCH, POOL_PAD, D_POOL)),
        'state_gla': n(3, (DEPTH, DEC_BATCH, GLA_HEADS, GLA_DK, GLA_DV)),
        'meta_tokens': n(4, (N_META, D_MODEL)),
        'norm_mix': 1.0 + 0.02 * n(5, (DEPTH, D_MODEL)),
        'w_in': n(6, (DEPTH, D_MODEL, D_IN)) * D_MODEL ** -0.5,
        'w_gate_up': n(7, (DEPTH, GATE_RANK, D_QK)) * GATE_RANK ** -0.5,
        'b_gate': 0.1 * n(8, (DEPTH, D_QK)),
        'w_pool': n(9, (DEPTH, N_POOL_GROUPS, POOL_GROUP_DIM, POOL_GROUP_DIM)) * POOL_GROUP_DIM ** -0.5,
        'pool_scale': 1.0 + 0.02 * n(10, (DEPTH, D_POOL)),
        'gla_norm': 1.0 + 0.02 * n(11, (DEPTH, D_V)),
        'w_out': n(12, (DEPTH, D_MIX, D_MODEL)) * D_MIX ** -0.5,
        'norm_ffn': 1.0 + 0.02 * n(13, (DEPTH, D_MODEL)),
        'w_router_group': n(14, (DEPTH, D_MODEL, N_GROUPS)) * D_MODEL ** -0.5,
        'b_router_group': 0.01 * n(15, (DEPTH, N_GROUPS)),
        'w_router_expert': n(16, (DEPTH, D_MODEL, N_EXPERTS)) * D_MODEL ** -0.5,
        'b_router_expert': 0.01 * n(17, (DEPTH, N_EXPERTS)),
        'w_expert_gate': n(18, (DEPTH, N_EXPERTS, D_MODEL, D_EXPERT)) * D_MODEL ** -0.5,
        'w_expert_up': n(19, (DEPTH, N_EXPERTS, D_MODEL, D_EXPERT)) * D_MODEL ** -0.5,
        'w_expert_down': n(20, (DEPTH, N_EXPERTS, D_EXPERT, D_MODEL)) * D_EXPERT ** -0.5,
        'norm_final': 1.0 + 0.02 * n(21, (D_MODEL,)),
    }

def reference(x_prompt, x_sample, state_pool, state_gla, meta_tokens, norm_mix, w_in, w_gate_up, b_gate,
              w_pool, pool_scale, gla_norm, w_out, norm_ffn, w_router_group, b_router_group,
              w_router_expert, b_router_expert, w_expert_gate, w_expert_up, w_expert_down, norm_final):
    B = x_prompt.shape[0]
    meta = jnp.broadcast_to(meta_tokens.astype(x_prompt.dtype)[None], (B, N_META, D_MODEL))
    hp = jnp.concatenate([meta, x_prompt], axis=1)
    hs = x_sample
    zero_pool = jnp.zeros((B, POOL_PAD, D_POOL), x_prompt.dtype)
    zero_gla = jnp.zeros((B, GLA_HEADS, GLA_DK, GLA_DV), jnp.float32)
    pool_p, gla_p, pool_s, gla_s = [], [], [], []
    for l in range(DEPTH):
        lw = (norm_mix[l], w_in[l], w_gate_up[l], b_gate[l], w_pool[l], pool_scale[l], gla_norm[l], w_out[l],
              norm_ffn[l], w_router_group[l], b_router_group[l], w_router_expert[l], b_router_expert[l],
              w_expert_gate[l], w_expert_up[l], w_expert_down[l])
        hp, sp, gp = encoder_layer(hp, zero_pool, 0, zero_gla, CHUNK, CHUNK - N_META, *lw)
        hs, ss, gs = encoder_layer(hs, state_pool[l], POOL_PAD, state_gla[l], hs.shape[1], 0, *lw)
        pool_p.append(sp)
        gla_p.append(gp)
        pool_s.append(ss)
        gla_s.append(gs)
    y_prompt = rmsnorm(hp[:, N_META:], norm_final).astype(x_prompt.dtype)
    y_sample = rmsnorm(hs, norm_final).astype(x_sample.dtype)
    return (y_prompt, y_sample, jnp.stack(pool_p), jnp.stack(gla_p), jnp.stack(pool_s), jnp.stack(gla_s))


_drawn_inputs = setup_inputs


def setup_inputs(seed=0):
    import zlib

    import numpy as np

    out = dict(_drawn_inputs(seed))
    spreads = {}
    factors = {'gla_norm': 8.667,
     'b_router_group': 64.0,
     'b_router_expert': 5.051,
     'norm_final': 7.523,
     'pool_scale': 5.149,
     'norm_ffn': 2.994}
    for name, (base, spread) in spreads.items():
        noise = np.random.default_rng([zlib.crc32(name.encode()), seed]).standard_normal(out[name].shape)
        drawn = base * np.exp(spread * noise) if base else spread * noise
        out[name] = __import__('jax').numpy.asarray(drawn.astype(out[name].dtype))
    for name, factor in factors.items():
        out[name] = (out[name] * factor).astype(out[name].dtype)
    return out
```

```python
from contextlib import ExitStack

import concourse.bass as bass
from concourse import mybir
import numpy as np

F32 = mybir.dt.float32
BF16 = mybir.dt.bfloat16
I32 = mybir.dt.int32
ALU = mybir.AluOpType
ACT = mybir.ActivationFunctionType
AX = mybir.AxisListType

P = 128
D = 1024
KD = D // P
SEQ = 1024
SAMPLE = 64
CHUNK = 64
META = 16
PADS = CHUNK - META
TILES = (SAMPLE + PADS + META + SEQ) // P
EPS = 1e-6
D_POOL = D // 2
WINDOWS = (2, 4, 8, 16)
NG = len(WINDOWS)
HIST = max(WINDOWS) - 1
HEADS = 4
DK = D // 16
DV = D // 8
PAIRS = HEADS // 2
D_QK = HEADS * DK
D_V = HEADS * DV
RANK = 16
TAU = 16.0
D_IN = D_POOL + 2 * D_QK + 2 * D_V + RANK
U0, Q0, K0, V0, R0, Z0 = (0, D_POOL, D_POOL + D_QK, D_POOL + 2 * D_QK, D_POOL + 2 * D_QK + D_V, D_POOL + 2 * D_QK + 2 * D_V)
GROUPS = 4
PER_GROUP = 8
NE = GROUPS * PER_GROUP
FF = D // 2
KF = FF // P
NL = GROUPS + NE
BLOCK = 96
TOKENS = SAMPLE + META + SEQ
PICKS = 2
EXTRA_PER_E = (TOKENS - 1) // BLOCK
EXTRA = (PICKS * TOKENS - 1) // BLOCK
SLOTS = (NE + EXTRA) * BLOCK
BIG = 3.0e38

_WIDTHS = [("ident", P), ("keep", PAIRS * P), ("causal", P), ("before", P), ("count_fix", NG * META),
           ("iota_block", BLOCK), ("iota_e", NE), ("first_g", GROUPS), ("first_e", PER_GROUP), ("token", 1),
           ("valid", 1), ("block_edge", EXTRA_PER_E), ("iota_x", EXTRA), ("edge_x", EXTRA)]
COL = {}
_at = 0
for _n, _w in _WIDTHS:
    COL[_n] = (_at, _at + _w)
    _at += _w
N_CONST = _at


def constants():
    c = np.zeros((P, N_CONST), np.float32)
    p = np.arange(P)[:, None]
    t = np.arange(P)[None, :]

    def put(name, v):
        c[:, COL[name][0]:COL[name][1]] = v

    put("ident", p == t)
    put("keep", np.arange(PAIRS * P)[None, :] % CHUNK != 0)
    put("causal", (p <= t) & (p // CHUNK == t // CHUNK))
    put("before", p < t)
    put("count_fix", np.concatenate([w / np.minimum(np.arange(META) + 1, w) for w in WINDOWS])[None, :])
    put("iota_block", np.arange(BLOCK)[None, :])
    put("iota_e", np.arange(NE)[None, :])
    put("first_g", GROUPS - np.arange(GROUPS)[None, :])
    put("first_e", PER_GROUP - np.arange(PER_GROUP)[None, :])
    put("token", p)
    put("valid", (p < SAMPLE) | (p >= SAMPLE + PADS))
    put("block_edge", BLOCK * (1 + np.arange(EXTRA_PER_E))[None, :])
    put("iota_x", np.arange(EXTRA)[None, :])
    put("edge_x", BLOCK * np.arange(EXTRA)[None, :])
    return c


def wait_parted(eng, sem, value, parted):
    eng.wait_ge(sem, value)
    if not isinstance(value, int):
        eng.sem_inc(parted, 1)


class Steps:

    def __init__(self, eng, sem):
        self.eng, self.sem, self.per, self.n, self.base = eng, sem, None, 0, 0

    def begin(self, i):
        self.n = 0
        self.base = i * self.per if self.per is not None else 0

    def __call__(self, ins):
        ins.then_inc(self.sem, 1)
        self.n += 1

    def settle(self):
        self.eng.wait_ge(self.sem, self.base + self.n)

    def then(self, ins):
        self(ins)
        self.settle()

    def end(self):
        assert self.per in (None, self.n)
        self.per = self.n


def build(nc, x_all, state_pool, state_gla, norm_mix, w_in, w_gate_up, b_gate, w_pool, pool_scale, gla_norm, w_out,
          norm_ffn, w_router, b_router, w_eg, w_eu, w_ed, norm_final, const,
          y_prompt, y_sample, pool_prompt, gla_prompt, pool_sample, gla_sample):
    hn_dram = nc.dram_tensor("hn_rows", (TILES * P, D), F32, kind="Internal").ap()
    ys_dram = nc.dram_tensor("expert_rows", (SLOTS, D), F32, kind="Internal").ap()

    with ExitStack() as ctx:
        def sb(name, shape, dt=F32):
            return ctx.enter_context(nc.sbuf_tensor(name, shape, dt))

        def sem(name):
            return ctx.enter_context(nc.semaphore(name))

        bank = [ctx.enter_context(nc.psum_tensor(f"bank{n}", [P, 512], F32)) for n in range(8)]

        arena = sb("arena", [P, KD * D_IN + KD * D])
        w_in_sb = arena[:, 0:KD * D_IN].rearrange("p (k n) -> p k n", k=KD)
        w_out_sb = arena[:, KD * D_IN:KD * D_IN + KD * D].rearrange("p (k n) -> p k n", k=KD)
        EW = KD * FF
        starts = {("g", 0): 0, ("u", 0): EW, ("d", 0): 2 * EW, ("g", 1): 3 * EW, ("u", 1): KD * D_IN, ("d", 1): KD * D_IN + EW}
        wg = [arena[:, starts["g", b]:starts["g", b] + EW].rearrange("p (k n) -> p k n", k=KD) for b in range(2)]
        wu = [arena[:, starts["u", b]:starts["u", b] + EW].rearrange("p (k n) -> p k n", k=KD) for b in range(2)]
        wd = [arena[:, starts["d", b]:starts["d", b] + EW].rearrange("p (k n) -> p k n", k=KF) for b in range(2)]

        cst = sb("cst", [P, N_CONST])

        def con(name, rows=P):
            return cst[0:rows, COL[name][0]:COL[name][1]]

        ident = con("ident")
        one_dv = sb("one_dv", [P, P])
        ZW = 256
        zeros = sb("zeros", [BLOCK, ZW])
        eps = sb("eps", [P, 1])
        ones_bf = sb("ones_bf", [P, P], BF16)
        before_bf = sb("before_bf", [P, P], BF16)
        causal_i = sb("causal_i", [P, P], I32)
        g_mix = sb("g_mix", [P, KD])
        g_ffn = sb("g_ffn", [P, KD])
        b_gate_sb = sb("b_gate_sb", [P, PAIRS])
        mix_scale = sb("mix_scale", [P, NG + HEADS])
        w_pool_sb = sb("w_pool_sb", [P, NG, P])
        w_up_sb = sb("w_up_sb", [RANK, D_QK])
        w_r_sb = sb("w_r_sb", [P, KD, NL])
        b_r_sb = sb("b_r_sb", [P, NL])

        h_all = sb("h_all", [P, TILES, D])
        xs = sb("xs", [P, KD, P])
        xss = sb("xss", [P, 1])
        xnT = sb("xnT", [P, KD, P])
        z_sb = sb("z_sb", [RANK, P])
        qk = sb("qk", [P, 2, PAIRS, P])
        gate_work = sb("gate_work", [P, 7, PAIRS, P])
        gx, ga, ge, eb, enb = (gate_work[:, n, :, :] for n in range(5))
        cum, dec = (gate_work[:, n, :, :].rearrange("p a n -> p (a n)") for n in (5, 6))
        q_i = sb("q_i", [P, HEADS, P])
        k_i = sb("k_i", [P, PAIRS, P])
        k_dec = sb("k_dec", [P, PAIRS, P])
        kz_v = sb("kz_v", [P, 2 * PAIRS * P + D_V])
        kz = kz_v[:, 0:2 * PAIRS * P].rearrange("p (c a n) -> p c a n", c=2, a=PAIRS)
        v_sb = kz_v[:, 2 * PAIRS * P:]
        sc = sb("sc", [P, HEADS, P])
        sA = sb("sA", [P, PAIRS, DV])
        sB = sb("sB", [P, PAIRS, DV])
        s_sample = sb("s_sample", [P, PAIRS, DV])
        window_work = sb("window_work", [P, 3, NG, HIST + P])
        u_ext, sum2, sum4 = (window_work[:, n, :, :] for n in range(3))
        pooled = sb("pooled", [P, NG, P])
        u_keep = sb("u_keep", [P, 2, NG, HIST])
        pool_out = [q_i[0:HIST, :, :].rearrange("p h n -> p (h n)"), sc[0:HIST, :, :].rearrange("p h n -> p (h n)")]
        er = sb("er", [P, HEADS, P])
        silu_r = sb("silu_r", [P, HEADS, P])
        osq = sb("osq", [P, HEADS, P])
        rs = er
        pool_in = osq[0:HIST, :, :].rearrange("p h n -> p (h n)")

        mixT = sb("mixT", [P, KD, P])
        hs = sb("hs", [P, KD, P])
        hss = sb("hss", [P, 1])
        hnT = sb("hnT", [P, KD, P])
        lg = sb("lg", [P, NL])
        rt = sb("rt", [P, 16])
        dG = sb("dG", [P, GROUPS])
        cG = sb("cG", [P, GROUPS])
        oG = sb("oG", [P, GROUPS])
        eG = sb("eG", [P, GROUPS])
        selE = sb("selE", [P, GROUPS, PER_GROUP])
        le = sb("le", [P, 4, PER_GROUP])
        oh = sb("oh", [P, PICKS, PER_GROUP])
        M = sb("M", [P, PICKS, GROUPS, PER_GROUP])
        M_bf = sb("M_bf", [P, NE], BF16)
        M_tok = sb("M_tok", [P, PICKS, NE])
        R = sb("R", [P, NE])
        prod = sb("prod", [P, PICKS, NE])
        prod_e = sb("prod_e", [P, PICKS, NE])
        at_rank = sb("at_rank", [P, PICKS, BLOCK])
        counts = sb("counts", [P, NE])
        token = sb("token", [P, 1])
        rk = sb("rk", [P, PICKS])
        rank_all = sb("rank_all", [P, TILES, PICKS])
        e_all = sb("e_all", [P, TILES, PICKS])
        gate_all = sb("gate_all", [P, TILES, PICKS])
        idx_f = sb("idx_f", [BLOCK, NE])
        idx_i = sb("idx_i", [BLOCK, NE], I32)

        NP = TILES * PICKS
        free_work = gate_work[:, :, :, :].rearrange("p s a n -> p (s a n)")
        at = [0, NP * NE, NP * NE + EXTRA * NE]
        is_e = free_work[:, at[0]:at[1]].rearrange("p (n e) -> p n e", e=NE)
        own_x = free_work[:, at[1]:at[2]].rearrange("p (n e) -> p n e", e=NE)
        over = free_work[:, 0:NE * EXTRA_PER_E].rearrange("p (e n) -> p e n", e=NE)
        n_extra = sb("n_extra", [P, NE])
        upto = sb("upto", [P, NE])
        base_e = sb("base_e", [P, NE])
        slot_f = sb("slot_f", [P, NP])
        slot_t = sb("slot_t", [P, 2, NP])
        slot_i = sb("slot_i", [P, NP], I32)
        steer = sb("steer", [1, 1 + EXTRA], I32)
        x_of = sb("x_of", [P, EXTRA])

        v_spare = kz_v[:, :]
        spare = window_work[:, :, :, :].rearrange("p s g n -> p (s g n)")
        rows = [spare[0:BLOCK, 0:D], xs[0:BLOCK, :, :].rearrange("p k n -> p (k n)")]
        rowsT = [xnT[:, :, 0:BLOCK], hnT[:, :, 0:BLOCK]]
        sig = mixT[:, 0:3, :].rearrange("p k n -> p (k n)")
        gs = mixT[:, 3:6, :].rearrange("p k n -> p (k n)")
        hid = [osq[:, 0:3, :].rearrange("p k n -> p (k n)"), silu_r[:, 0:3, :].rearrange("p k n -> p (k n)")]
        ye = [v_spare[0:BLOCK, :], hs[0:BLOCK, :, :].rearrange("p k n -> p (k n)")]
        NH = KF * BLOCK
        assert NH <= 3 * P
        rows_idx = [sb(f"rows_idx{b}", [BLOCK, 1], I32) for b in range(2)]
        idx_xf = sb("idx_xf", [BLOCK, EXTRA])
        idx_xi = sb("idx_xi", [BLOCK, EXTRA], I32)
        x_lo = sb("x_lo", [P, EXTRA])
        x_hi = sb("x_hi", [P, EXTRA])
        x_at = sb("x_at", [P, 4])

        def lot(n):
            return arena[:, n * D:(n + 1) * D]
        y1 = [lot(2 * i) for i in range(TILES)]
        y2 = [lot(2 * i + 1) for i in range(TILES)]
        g_fin = lot(2 * TILES)
        fss = sb("fss", [P, TILES])

        names = ("""consts_in first_small_in small_in history_in x0_in x1_in x_rest_in w_z_in w_qk_in w_u_in w_r_in w_v_in
            w_out_in w_out_scaled hn_stored
            pe_xT pe_z pe_gate pe_qk pe_u pe_r pe_v pe_pool pe_kT pe_scores pe_kvA pe_kvB pe_o pe_ones pe_wout pe_hT
            pe_router pe_rank pe_idx pe_hist_T pe_small_T
            setup_dve setup_pool z_ready qk_ready ge_ready eb_ready enb_ready edec_ready u_ready er_ready v_ready kz_ready
            osq_ready rs_ready xs_ready hs_ready rexp_ready
            xnT_ready ga_ready cum_ready dec_ready qi_ready ki_ready kdec_ready sums_ready pooled_ready silu_ready
            mixp_ready mixo_ready h_added hnT_ready logits_ready routes_ready onehot_ready sc_ready sB_ready sA_ready idx_added
            u_kept s_sample_ready pool_out_ready outs_stored zeros_stored idx_ready slots_ready
            parted dve_front dve_back dve_once dve_moe dve_fin act_front act_back act_once act_fin history_kept pool_steps
            pe_eT pe_g pe_u2 pe_d0 pe_d sig_ready hid_ready eT_ready ye_ready row_idx_ready
            x_tab_dve x_tab_pe x_idx_ready x_w x_rows x_pe x_dve x_act x_stored x_pool
            fin_ready frstd_ready out_ready g_fin_in""").split()
        s = {n: sem(n) for n in names}
        g_in = [sem(f"g_in{b}") for b in range(2)]
        u_in = [sem(f"u_in{b}") for b in range(2)]
        d_in = [sem(f"d_in{b}") for b in range(2)]
        rows_in = [sem(f"rows_in{b}") for b in range(2)]
        ye_stored = [sem(f"ye_stored{b}") for b in range(2)]
        y_in = [sem(f"y_in{i}") for i in range(TILES)]

        w_in_v = w_in.rearrange("(p k) n -> p k n", k=KD)
        SMALL, FIRST_SMALL = 12, 4
        TABLE_STEPS = 10
        X_STEPS = 6
        block = ctx.enter_context(nc.Block())

        @block.sync
        def _(sp):
            x_tiles = x_all.rearrange("(t p) n -> p t n", p=P)
            sp.dma_start(h_all[:, 0, :], x_tiles[:, 0, :]).then_inc(s["x0_in"], 16)
            sp.dma_start(cst[:, :], const).then_inc(s["consts_in"], 16)
            small = [
                (g_mix[:, :], norm_mix.rearrange("(p k) -> p k", k=KD)),
                (g_ffn[:, :], norm_ffn.rearrange("(p k) -> p k", k=KD)),
                (b_gate_sb[:, :], b_gate.rearrange("(g p) -> p g", p=P)),
                (w_up_sb[:, :], w_gate_up),
                (pool_in, state_pool),
                (sA[:, 0, :], state_gla[0:2].rearrange("h k v -> (h k) v")),
                (sA[:, 1, :], state_gla[2:4].rearrange("h k v -> (h k) v")),
                (mix_scale[:, 0:NG], pool_scale.rearrange("(g p) -> p g", p=P)),
                (mix_scale[:, NG:], gla_norm.rearrange("(g p) -> p g", p=P)),
                (w_pool_sb[:, :, :], w_pool.rearrange("g c d -> c g d")),
                (w_r_sb[:, :, :], w_router.rearrange("(p k) n -> p k n", k=KD)),
                (b_r_sb[:, :], b_router.partition_broadcast(P)),
            ]
            assert len(small) == SMALL
            def load_w_in(name, a, b):
                sp.dma_start(w_in_sb[:, :, a:b], w_in_v[:, :, a:b]).then_inc(s[name], 16)

            with nc.allow_non_contiguous_dma("vectors of a few elements per partition"):
                for out, src in small[:FIRST_SMALL]:
                    sp.dma_start(out, src).then_inc(s["first_small_in"], 16)
                load_w_in("w_z_in", Z0, D_IN)
                load_w_in("w_qk_in", Q0, V0)
                load_w_in("w_u_in", U0, Q0)
                for out, src in small[FIRST_SMALL:]:
                    sp.dma_start(out, src).then_inc(s["small_in"], 16)
                load_w_in("w_r_in", R0, Z0)
                sp.dma_start(h_all[:, 1, :], x_tiles[:, 1, :]).then_inc(s["x1_in"], 16)
                load_w_in("w_v_in", V0, R0)
            sp.dma_start(w_out_sb, w_out.rearrange("(k p) n -> p k n", p=P)).then_inc(s["w_out_in"], 16)

            sp.dma_start(h_all[:, 2:, :], x_tiles[:, 2:, :]).then_inc(s["x_rest_in"], 16)
            sp.wait_ge(s["setup_pool"], 5)
            sp.dma_start(ys_dram[NE * BLOCK:, :].rearrange("(p b) (c n) -> p (b c) n", p=BLOCK, n=ZW),
                         zeros[:, :].unsqueeze(1).to_broadcast([BLOCK, EXTRA * D // ZW, ZW])).then_inc(s["zeros_stored"], 16)
            sp.wait_ge(s["s_sample_ready"], 1)
            with nc.allow_non_contiguous_dma("state of the sample"):
                for p in range(PAIRS):
                    sp.dma_start(gla_sample[2 * p:2 * p + 2].rearrange("h k v -> (h k) v"), s_sample[:, p, :]).then_inc(s["outs_stored"], 16)

            def load_weights(t, b):
                e = 2 * t + b
                sp.dma_start(wg[b], w_eg[bass.ds(e * D, D), :].rearrange("(p k) n -> p k n", k=KD)).then_inc(g_in[b], 16)
                if isinstance(t, int) and b == 1:
                    sp.wait_ge(s["pe_wout"], TILES)
                if not isinstance(t, int):
                    sp.wait_ge(s["pe_u2"], 2 * (e - 1))
                sp.dma_start(wu[b], w_eu[bass.ds(e * D, D), :].rearrange("(p k) n -> p k n", k=KD)).then_inc(u_in[b], 16)
                if not isinstance(t, int):
                    sp.wait_ge(s["pe_d"], e - 1)
                sp.dma_start(wd[b], w_ed[bass.ds(e * FF, FF), :].rearrange("(k p) n -> p k n", p=P)).then_inc(d_in[b], 16)

            sp.wait_ge(s["pe_v"], TILES)
            load_weights(0, 0)
            load_weights(0, 1)
            sp.wait_ge(s["sA_ready"], TILES)
            for p in range(PAIRS):
                sp.dma_start(gla_prompt[2 * p:2 * p + 2].rearrange("h k v -> (h k) v"), sA[:, p, :]).then_inc(s["outs_stored"], 16)
            sp.wait_ge(s["pool_out_ready"], 2)
            sp.dma_start(pool_sample, pool_out[0]).then_inc(s["outs_stored"], 16)
            sp.dma_start(pool_prompt, pool_out[1]).then_inc(s["outs_stored"], 16)
            with sp.Fori(1, NE // 2) as t:
                for b in range(2):
                    sp.wait_ge(s["pe_g"], 2 * t + b - 1)
                    load_weights(t, b)

            sp.wait_ge(s["slots_ready"], 1)
            n_x = sp.value_load(steer[0:1, 0:1], min_val=0, max_val=EXTRA)
            sp.wait_ge(s["pe_d"], NE)
            with sp.If(n_x > 0):
                with sp.Fori(0, EXTRA) as n:
                    with sp.If(n < n_x):
                        e = sp.value_load(steer[0:1, bass.ds(n + 1, 1)], min_val=0, max_val=NE - 1)
                        sp.dma_start(wg[0], w_eg[bass.ds(e * D, D), :].rearrange("(p k) n -> p k n", k=KD)).then_inc(s["x_w"], 16)
                        sp.dma_start(wu[0], w_eu[bass.ds(e * D, D), :].rearrange("(p k) n -> p k n", k=KD)).then_inc(s["x_w"], 16)
                        sp.dma_start(wd[0], w_ed[bass.ds(e * FF, FF), :].rearrange("(k p) n -> p k n", p=P)).then_inc(s["x_w"], 16)
                        wait_parted(sp, s["x_stored"], 16 * n + 16, s["parted"])
            sp.dma_start(g_fin, norm_final.partition_broadcast(P)).then_inc(s["g_fin_in"], 16)
            for i in range(TILES):
                sp.wait_ge(s["out_ready"], i + 1)
                if i == 0:
                    sp.dma_start(y_sample, y2[i][0:SAMPLE, :]).then_inc(s["outs_stored"], 16)
                else:
                    sp.dma_start(y_prompt[(i - 1) * P:i * P, :], y2[i]).then_inc(s["outs_stored"], 16)
            sp.wait_ge(s["outs_stored"], 16 * (2 * PAIRS + 2 + TILES))

        @block.gpsimd
        def _(pool):
            pool.memset(q_i[:, :, :], 0.0).then_inc(s["setup_pool"], 1)
            pool.memset(kz[:, :, :, :], 0.0).then_inc(s["setup_pool"], 1)
            pool.memset(sc[:, :, :], 0.0).then_inc(s["setup_pool"], 1)
            pool.memset(sB[:, :, :], 0.0).then_inc(s["setup_pool"], 1)
            pool.memset(zeros[:, :], 0.0).then_inc(s["setup_pool"], 1)

            def windows(i, first=False):
                pool.wait_ge(s["u_ready"], i + 1)
                w = HIST + P
                g = s["pool_steps"]
                nc.gpsimd.tensor_tensor(sum2[:, :, 1:w], u_ext[:, :, 1:w], u_ext[:, :, 0:w - 1], ALU.add).then_inc(g, 1)
                pool.wait_ge(g, 3 * i + 1)
                nc.gpsimd.tensor_tensor(sum4[:, 1:, 3:w], sum2[:, 1:, 3:w], sum2[:, 1:, 1:w - 2], ALU.add).then_inc(g, 1)
                pool.wait_ge(g, 3 * i + 2)
                nc.gpsimd.tensor_tensor(sum2[:, 2:, 7:w], sum4[:, 2:, 7:w], sum4[:, 2:, 3:w - 4], ALU.add).then_inc(g, 1)
                pool.wait_ge(g, 3 * i + 3)
                nc.gpsimd.tensor_tensor(sum4[:, 3:, 15:w], sum2[:, 3:, 15:w], sum2[:, 3:, 7:w - 8], ALU.add).then_inc(s["sums_ready"], 1)

            pool.wait_ge(s["history_in"], 1)
            windows(0)
            with pool.Fori(1, TILES) as i:
                windows(i)

            pool.wait_ge(s["idx_ready"], 1)
            pool.wait_ge(s["hn_stored"], 16 * TILES)

            def gather(t, b):
                e = 2 * t + b
                nc.gpsimd.tensor_copy(rows_idx[b][:, :], idx_i[:, bass.ds(e, 1)]).then_inc(s["row_idx_ready"], 1)
                wait_parted(pool, s["row_idx_ready"], e + 1, s["parted"])
                nc.gpsimd.indirect_dma_start(rows[b], None, hn_dram, bass.IndirectOffsetOnAxis(ap=rows_idx[b][:, :], axis=0),
                                             bounds_check=TILES * P - 1).then_inc(rows_in[b], 16)

            gather(0, 0)
            gather(0, 1)
            with pool.Fori(1, NE // 2) as t:
                for b in range(2):
                    wait_parted(pool, s["pe_eT"], 2 * t + b - 1, s["parted"])
                    gather(t, b)

            pool.wait_ge(s["slots_ready"], 1)
            n_x = pool.value_load(steer[0:1, 0:1], min_val=0, max_val=EXTRA)
            pool.wait_ge(s["x_idx_ready"], 1)
            pool.wait_ge(s["pe_eT"], NE)
            with pool.If(n_x > 0):
                with pool.Fori(0, EXTRA) as n:
                    with pool.If(n < n_x):
                        nc.gpsimd.tensor_copy(rows_idx[0][:, :], idx_xi[:, bass.ds(n, 1)]).then_inc(s["x_pool"], 1)
                        wait_parted(pool, s["x_pool"], n + 1, s["parted"])
                        nc.gpsimd.indirect_dma_start(rows[0], None, hn_dram, bass.IndirectOffsetOnAxis(ap=rows_idx[0][:, :], axis=0),
                                                     bounds_check=TILES * P - 1).then_inc(s["x_rows"], 16)
                        wait_parted(pool, s["x_stored"], 16 * n + 16, s["parted"])

            for b in range(2):
                pool.wait_ge(ye_stored[b], 16 * (NE // 2))
            pool.wait_ge(s["zeros_stored"], 16)
            pool.wait_ge(s["pe_d"], NE)

            for i in range(TILES):
                for y, k in ((y1[i], 0), (y2[i], 1)):
                    nc.gpsimd.indirect_dma_start(y, None, ys_dram,
                                                 bass.IndirectOffsetOnAxis(ap=slot_i[:, i * PICKS + k:i * PICKS + k + 1], axis=0),
                                                 bounds_check=SLOTS - 1).then_inc(y_in[i], 16)

        @block.scalar
        def _(act):
            A = nc.scalar.activation
            front = Steps(act, s["act_front"])
            back = Steps(act, s["act_back"])
            once = Steps(act, s["act_once"])
            final = Steps(act, s["act_fin"])

            def rstd(steps, x, squares, out):
                steps.then(A(squares, x, ACT.Square, scale=D ** -0.5, accum_out=out))
                steps.then(A(out, out, ACT.Ln, bias=eps[:, 0:1]))
                steps(A(out, out, ACT.Exp, scale=-0.5))
                wait_parted(act, steps.sem, steps.base + steps.n, s["parted"])

            def x_scale(steps, i, first=False):
                x = h_all[:, bass.ds(i, 1), :]
                if not first:
                    wait_parted(act, s["pe_xT"], 2 * i, s["parted"])
                rstd(steps, x.rearrange("p a n -> p (a n)"), xs[:, :, :].rearrange("p k n -> p (k n)"), xss[:, 0:1])
                A(xs[:, :, :], x.rearrange("t a (p k) -> t (a k) p", k=KD), ACT.Copy, scale=xss[:, 0:1]).then_inc(s["xs_ready"], 1)

            def scale_w_out(a, b):
                for k in range(a, b):
                    A(w_out_sb[:, k, :], w_out_sb[:, k, :], ACT.Copy, scale=mix_scale[:, k:k + 1]).then_inc(s["w_out_scaled"], 1)

            def front_gates(i, first=False, second=False):
                act.wait_ge(s["pe_z"], i + 1)
                if not first:
                    act.wait_ge(s["pe_gate"], i)
                A(z_sb[:, :], bank[3][0:RANK, 0:P], ACT.Copy).then_inc(s["z_ready"], 1)
                if second:
                    scale_w_out(2, KD - 1)
                act.wait_ge(s["pe_qk"], i + 1)
                if not first:
                    act.wait_ge(s["kdec_ready"], i)
                A(qk[:, :, :, :].rearrange("p a b n -> p (a b n)"), bank[2][:, :], ACT.Copy).then_inc(s["qk_ready"], 1)
                act.wait_ge(s["ga_ready"], i + 1)
                front.then(A(ge[:, :, :], ga[:, :, :], ACT.Exp, scale=-1.0))
                A(ge[:, :, :], ge[:, :, :], ACT.Ln, bias=1.0).then_inc(s["ge_ready"], 1)
                act.wait_ge(s["cum_ready"], i + 1)
                A(eb[:, :, :].rearrange("p a n -> p (a n)"), cum[:, :], ACT.Exp, scale=1.0 / TAU).then_inc(s["eb_ready"], 1)
                A(enb[:, :, :].rearrange("p a n -> p (a n)"), cum[:, :], ACT.Exp, scale=-1.0 / TAU).then_inc(s["enb_ready"], 1)
                act.wait_ge(s["dec_ready"], i + 1)
                A(dec[:, :], dec[:, :], ACT.Exp, scale=1.0 / TAU).then_inc(s["edec_ready"], 1)

            def front_u(i, first=False):
                if not first:
                    act.wait_ge(s["pooled_ready"], i)
                    act.wait_ge(s["u_kept"], 1)
                    A(u_ext[:, :, 0:HIST], u_ext[:, :, P:P + HIST], ACT.Copy).then_inc(s["history_kept"], 1)
                    act.wait_ge(s["history_kept"], i)
                act.wait_ge(s["pe_u"], i + 1)
                A(u_ext[:, :, HIST:HIST + P], bank[4][:, :].rearrange("p (g n) -> p g n", g=NG), ACT.Copy).then_inc(s["u_ready"], 1)

            def front_r(i, first=False):
                act.wait_ge(s["pe_r"], i + 1)
                if not first:
                    act.wait_ge(s["mixo_ready"], i)
                A(er[:, :, :].rearrange("p h n -> p (h n)"), bank[5][:, :], ACT.Exp, scale=-1.0).then_inc(s["er_ready"], 1)

            def front_end(i, first=False):
                act.wait_ge(s["pe_v"], i + 1)
                if not first:
                    act.wait_ge(s["pe_o"], i)
                A(v_sb[:, :], bank[6][:, :], ACT.Copy).then_inc(s["v_ready"], 1)
                act.wait_ge(s["pe_pool"], i + 1)
                if not first:
                    act.wait_ge(s["pe_wout"], i)
                A(mixT[:, 0:NG, :].rearrange("p g n -> p (g n)"), bank[4][:, :], ACT.Copy).then_inc(s["mixp_ready"], 1)
                act.wait_ge(s["pe_kT"], i + 1)
                act.wait_ge(s["setup_pool"], 4)
                kt = bank[2][:, 0:PAIRS * P].rearrange("t (a n) -> t a n", a=PAIRS)
                A(kz[0:CHUNK, 0, :, :], kt[0:CHUNK], ACT.Copy).then_inc(s["kz_ready"], 1)
                A(kz[CHUNK:P, 1, :, :], kt[CHUNK:P], ACT.Copy).then_inc(s["kz_ready"], 1)
                act.wait_ge(s["pe_o"], i + 1)
                if not first:
                    act.wait_ge(s["pe_ones"], i)
                A(osq[:, :, :].rearrange("p h n -> p (h n)"), bank[4][:, :], ACT.Square).then_inc(s["osq_ready"], 1)

            def back_h(j, first=False):
                act.wait_ge(s["h_added"], j + 1)
                if not first:
                    act.wait_ge(s["pe_hT"], 2 * j)
                    wait_parted(act, s["hn_stored"], 16 * j, s["parted"])
                h = h_all[:, bass.ds(j, 1), :]
                rstd(back, h.rearrange("p a n -> p (a n)"), hs[:, :, :].rearrange("p k n -> p (k n)"), hss[:, 0:1])
                A(hs[:, :, :], h.rearrange("t a (p k) -> t (a k) p", k=KD), ACT.Copy, scale=hss[:, 0:1]).then_inc(s["hs_ready"], 1)
                act.wait_ge(s["hs_ready"], j + 1)
                act.dma_start(hn_dram[bass.ds(j * P, P), :], hs[:, :, :].rearrange("p k n -> p (k n)")).then_inc(s["hn_stored"], 16)

            def back_o(j):
                act.wait_ge(s["pe_ones"], j + 1)
                flat = rs[:, :, :].rearrange("p h n -> p (h n)")
                back.then(A(flat, bank[5][:, :], ACT.Ln, bias=eps[:, 0:1]))
                A(flat, flat, ACT.Exp, scale=-0.5).then_inc(s["rs_ready"], 1)

            def back_router(j):
                act.wait_ge(s["logits_ready"], j + 1)
                A(eG[:, :], dG[:, :], ACT.Exp, accum_out=rt[:, 8:9]).then_inc(s["rexp_ready"], 1)
                A(rt[:, 9:10], rt[:, 7:8], ACT.Exp).then_inc(s["rexp_ready"], 1)

            def body(i, first=False, last=False, second=False):
                front.begin(i)
                if not first:
                    back.begin(i - 1)
                    back_o(i - 1)
                front_gates(i, first, second)
                if second:
                    scale_w_out(KD - 1, KD)
                front_u(i, first)
                if not first:
                    back_h(i - 1, second)
                    back.end()
                front_r(i, first)
                if first:
                    act.wait_ge(s["x1_in"], 16)
                if second:
                    act.wait_ge(s["x_rest_in"], 16)
                if not last:
                    x_scale(front, i + 1)
                if not first:
                    back_router(i - 1)
                front_end(i, first)
                if not last:
                    front.end()

            nc.scalar.preload_act_table_set("natural_log_exp_and_others")
            act.wait_ge(s["x0_in"], 16)
            act.wait_ge(s["setup_dve"], 4)
            x_scale(once, 0, True)
            body(0, first=True)
            act.wait_ge(s["w_out_in"], 16)
            act.wait_ge(s["small_in"], 16 * (SMALL - FIRST_SMALL))
            scale_w_out(0, 2)
            body(1, second=True)
            with act.Fori(2, TILES - 1) as i:
                body(i)
            body(TILES - 1, last=True)
            back.begin(TILES - 1)
            back_o(TILES - 1)
            back_h(TILES - 1)
            back_router(TILES - 1)

            def expert(t, b, first=False):
                e = 2 * t + b
                act.wait_ge(s["pe_g"], e + 1)
                if not (first and b == 0):
                    act.wait_ge(s["hid_ready"], 2 * e)
                A(sig[:, 0:NH], bank[2 + b][:, 0:NH], ACT.Exp, scale=-1.0).then_inc(s["sig_ready"], 1)
                for half in range(2):
                    act.wait_ge(s["pe_d"] if half else s["pe_d0"], e + 1)
                    if half == 0 and not first:
                        act.wait_ge(ye_stored[b], 16 * t)
                    A(ye[b][:, half * 512:half * 512 + 512], bank[6 + half][0:BLOCK, :], ACT.Copy).then_inc(s["ye_ready"], 1)
                act.wait_ge(s["ye_ready"], 2 * e + 2)
                act.dma_start(ys_dram[bass.ds(e * BLOCK, BLOCK), :], ye[b]).then_inc(ye_stored[b], 16)

            act.wait_ge(s["hn_stored"], 16 * TILES)
            expert(0, 0, True)
            expert(0, 1, True)
            with act.Fori(1, NE // 2) as t:
                expert(t, 0)
                expert(t, 1)

            act.wait_ge(s["slots_ready"], 1)
            n_x = act.value_load(steer[0:1, 0:1], min_val=0, max_val=EXTRA)
            act.wait_ge(s["hid_ready"], 2 * NE)
            act.wait_ge(ye_stored[0], 16 * (NE // 2))
            act.wait_ge(s["zeros_stored"], 16)
            with act.If(n_x > 0):
                with act.Fori(0, EXTRA) as n:
                    with act.If(n < n_x):
                        act.wait_ge(s["x_pe"], 4 * n + 2)
                        A(sig[:, 0:NH], bank[2][:, 0:NH], ACT.Exp, scale=-1.0).then_inc(s["x_act"], 1)
                        act.wait_ge(s["x_pe"], 4 * n + 4)
                        for half in range(2):
                            A(ye[0][:, half * 512:half * 512 + 512], bank[6 + half][0:BLOCK, :], ACT.Copy).then_inc(s["x_act"], 1)
                        act.wait_ge(s["x_act"], 3 * n + 3)
                        act.dma_start(ys_dram[bass.ds((n + NE) * BLOCK, BLOCK), :], ye[0]).then_inc(s["x_stored"], 16)
                        wait_parted(act, s["x_stored"], 16 * n + 16, s["parted"])

            for i in range(TILES):
                act.wait_ge(s["fin_ready"], i + 1)
                final.then(A(y2[i], y1[i], ACT.Square, scale=D ** -0.5, accum_out=fss[:, i:i + 1]))
                final.then(A(fss[:, i:i + 1], fss[:, i:i + 1], ACT.Ln, bias=eps[:, 0:1]))
                A(fss[:, i:i + 1], fss[:, i:i + 1], ACT.Exp, scale=-0.5).then_inc(s["frstd_ready"], 1)

        @block.vector
        def _(dve):
            V = nc.vector
            front = Steps(dve, s["dve_front"])
            back = Steps(dve, s["dve_back"])
            once = Steps(dve, s["dve_once"])

            V.memset(one_dv[:, :], 1.0 / DV).then_inc(s["setup_dve"], 1)
            V.memset(ones_bf[:, :], 1.0).then_inc(s["setup_dve"], 1)
            V.memset(counts[:, :], 0.0).then_inc(s["setup_dve"], 1)
            V.memset(eps[:, :], EPS).then_inc(s["setup_dve"], 1)
            dve.wait_ge(s["consts_in"], 16)
            V.tensor_copy(before_bf[:, :], con("before")).then_inc(s["setup_dve"], 1)
            V.tensor_copy(causal_i[:, :], con("causal")).then_inc(s["setup_dve"], 1)
            V.tensor_copy(token[:, :], con("token")).then_inc(s["setup_dve"], 1)
            V.memset(idx_f[:, :], 0.0).then_inc(s["idx_added"], 1)
            def x_turned(i, first=False):
                if not first:
                    dve.wait_ge(s["pe_v"], i)
                for half in range(2):
                    dve.wait_ge(s["pe_xT"], 2 * i + half + 1)
                    k = slice(half * KD // 2, (half + 1) * KD // 2)
                    V.tensor_tensor(xnT[:, k, :], bank[half][:, :].rearrange("p (k n) -> p k n", n=P),
                                    g_mix[:, k].unsqueeze(2).to_broadcast([P, KD // 2, P]), ALU.mult).then_inc(s["xnT_ready"], 1)

            def front_gates(i, first=False):
                dve.wait_ge(s["pe_gate"], i + 1)
                pre = bank[3][:, P:P + PAIRS * P].rearrange("p (a n) -> p a n", a=PAIRS)
                bias = b_gate_sb[:, :].unsqueeze(2).to_broadcast([P, PAIRS, P])
                front.then(V.tensor_tensor(gx[:, :, :], pre, bias, ALU.add))
                V.scalar_tensor_tensor(out=ga[:, :, :], in0=gx[:, :, :], scalar=-1.0, in1=gx[:, :, :], op0=ALU.mult, op1=ALU.max).then_inc(s["ga_ready"], 1)
                dve.wait_ge(s["ge_ready"], i + 1)
                front.then(V.scalar_tensor_tensor(out=gx[:, :, :], in0=gx[:, :, :], scalar=0.0, in1=ge[:, :, :], op0=ALU.min, op1=ALU.subtract))
                V.tensor_tensor_scan(cum[:, :], con("keep"), gx[:, :, :].rearrange("p a n -> p (a n)"), 0.0,
                                     ALU.mult, ALU.add).then_inc(s["cum_ready"], 1)
                dve.wait_ge(s["cum_ready"], i + 1)
                by_chunk = cum[:, :].rearrange("p (c n) -> p c n", n=CHUNK)
                NC2 = PAIRS * P // CHUNK
                V.tensor_tensor(dec[:, :].rearrange("p (c n) -> p c n", n=CHUNK),
                                by_chunk[:, :, CHUNK - 1:CHUNK].to_broadcast([P, NC2, CHUNK]), by_chunk, ALU.subtract).then_inc(s["dec_ready"], 1)
                dve.wait_ge(s["qk_ready"], i + 1)
                dve.wait_ge(s["eb_ready"], i + 1)
                if first:
                    dve.wait_ge(s["setup_pool"], 4)
                else:
                    dve.wait_ge(s["pe_o"], i)
                for r in range(2):
                    rows_ = slice(r * DK, (r + 1) * DK)
                    V.scalar_tensor_tensor(out=q_i[rows_, r::2, :], in0=qk[rows_, 0, :, :], scalar=float(DK) ** -0.5,
                                           in1=eb[rows_, :, :], op0=ALU.mult, op1=ALU.mult).then_inc(s["qi_ready"], 1)
                dve.wait_ge(s["enb_ready"], i + 1)
                V.tensor_tensor(k_i[:, :, :], qk[:, 1, :, :], enb[:, :, :], ALU.mult).then_inc(s["ki_ready"], 1)
                dve.wait_ge(s["edec_ready"], i + 1)
                V.tensor_tensor(k_dec[:, :, :], qk[:, 1, :, :], dec[:, :].rearrange("p (a n) -> p a n", a=PAIRS), ALU.mult).then_inc(s["kdec_ready"], 1)

            def front_pool(i, first=False):
                dve.wait_ge(s["sums_ready"], i + 1)
                if not first:
                    dve.wait_ge(s["pe_pool"], i)
                else:
                    fix = con("count_fix").rearrange("p (g n) -> p g n", g=NG)
                    for g in range(NG):
                        w = (sum2 if g in (0, 2) else sum4)[:, g, HIST + P - META:HIST + P]
                        once.then(V.tensor_tensor(w, w, fix[:, g, :], ALU.mult))
                for g in range(NG):
                    src = sum2 if g in (0, 2) else sum4
                    ins = V.scalar_tensor_tensor(out=pooled[:, g, :], in0=src[:, g, HIST:], scalar=1.0 / WINDOWS[g],
                                                 in1=u_ext[:, g, HIST:], op0=ALU.mult, op1=ALU.subtract)
                    if g < NG - 1:
                        front(ins)
                    else:
                        ins.then_inc(s["pooled_ready"], 1)

            def front_silu(i):
                dve.wait_ge(s["er_ready"], i + 1)
                flat = er[:, :, :].rearrange("p h n -> p (h n)")
                front.then(V.tensor_scalar(flat, flat, 1.0, None, ALU.add))
                front.then(V.reciprocal(flat, flat))
                V.tensor_tensor(silu_r[:, :, :].rearrange("p h n -> p (h n)"), bank[5][:, :], flat, ALU.mult).then_inc(s["silu_ready"], 1)

            def update(out, state, last_col, kv, signal):
                for r in range(2):
                    for p in range(PAIRS):
                        rows_ = slice(r * DK, (r + 1) * DK)
                        ins = V.scalar_tensor_tensor(out=out[rows_, p, :], in0=state[rows_, p, :], scalar=eb[rows_, p, last_col:last_col + 1],
                                                     in1=kv[rows_, (2 * p + r) * DV:(2 * p + r + 1) * DV], op0=ALU.mult, op1=ALU.add)
                        if r and p == PAIRS - 1:
                            ins.then_inc(signal, 1)
                        else:
                            front(ins)

            def front_gla(i, first=False):
                wait_parted(dve, s["pe_scores"], i + 1, s["parted"])
                V.copy_predicated(sc[:, :, :], causal_i[:, :].unsqueeze(1).to_broadcast([P, HEADS, P]),
                                  bank[5][:, :].rearrange("p (h n) -> p h n", h=HEADS)).then_inc(s["sc_ready"], 1)
                dve.wait_ge(s["pe_kvA"], i + 1)
                if first:
                    update(s_sample, sA, CHUNK - 1, bank[3], s["s_sample_ready"])
                    V.tensor_copy(u_keep[:, 0, :, :], u_ext[:, :, SAMPLE:SAMPLE + HIST]).then_inc(s["u_kept"], 1)
                else:
                    update(sB, sA, CHUNK - 1, bank[3], s["sB_ready"])

            def front_state(i, first=False):
                dve.wait_ge(s["pe_o"], i + 1)
                dve.wait_ge(s["pe_kvB"], i + 1)
                if not first:
                    dve.wait_ge(s["sB_ready"], i)
                    front.settle()
                update(sA, sB, P - 1, bank[6], s["sA_ready"])

            def back_o(j, first=False):
                dve.wait_ge(s["rs_ready"], j + 1)
                flat = rs[:, :, :].rearrange("p h n -> p (h n)")
                back.then(V.tensor_tensor(flat, flat, silu_r[:, :, :].rearrange("p h n -> p (h n)"), ALU.mult))
                V.tensor_tensor(mixT[:, NG:, :].rearrange("p h n -> p (h n)"), bank[4][:, :], flat, ALU.mult).then_inc(s["mixo_ready"], 1)

            def back_h(j):
                dve.wait_ge(s["pe_wout"], j + 1)
                h = h_all[:, bass.ds(j, 1), :].rearrange("p a n -> p (a n)")
                back(V.tensor_tensor(h[:, 0:512], bank[0][:, :], h[:, 0:512], ALU.add))
                V.tensor_tensor(h[:, 512:D], bank[1][:, :], h[:, 512:D], ALU.add).then_inc(s["h_added"], 1)

            def back_turned(j, first=False):
                if not first:
                    dve.wait_ge(s["pe_router"], j)
                for half in range(2):
                    dve.wait_ge(s["pe_hT"], 2 * j + half + 1)
                    k = slice(half * KD // 2, (half + 1) * KD // 2)
                    V.tensor_tensor(hnT[:, k, :], bank[half][:, :].rearrange("p (k n) -> p k n", n=P),
                                    g_ffn[:, k].unsqueeze(2).to_broadcast([P, KD // 2, P]), ALU.mult).then_inc(s["hnT_ready"], 1)

            def first_of(step, values, top, order, marks, out, valid=None):
                step.then(V.tensor_reduce(top, values, AX.X, ALU.max))
                step.then(V.scalar_tensor_tensor(out=marks, in0=values, scalar=top, in1=order, op0=ALU.is_ge, op1=ALU.mult))
                step.then(V.tensor_reduce(rt[:, 0:1], marks, AX.X, ALU.max))
                if valid is None:
                    step.then(V.tensor_scalar(out, marks, rt[:, 0:1], None, ALU.is_equal))
                else:
                    step.then(V.tensor_scalar(out, marks, rt[:, 0:1], valid, ALU.is_equal, ALU.mult))

            def back_route(j, first=False):
                dve.wait_ge(s["pe_router"], j + 1)
                back.then(V.tensor_tensor(lg[:, :], bank[7][:, 0:NL], b_r_sb[:, :], ALU.add))
                first_of(back, lg[:, 0:GROUPS], rt[:, 1:2], con("first_g"), cG[:, :], oG[:, :], con("valid") if first else None)
                back(V.tensor_scalar(dG[:, :], lg[:, 0:GROUPS], rt[:, 1:2], None, ALU.subtract))
                back.then(V.tensor_tensor(selE[:, :, :], lg[:, GROUPS:].rearrange("p (g e) -> p g e", g=GROUPS),
                                          oG[:, :].unsqueeze(2).to_broadcast([P, GROUPS, PER_GROUP]), ALU.mult))
                back.then(V.tensor_reduce(le[:, 0, :], selE[:, :, :].rearrange("p g e -> p e g"), AX.X, ALU.add))
                first_of(back, le[:, 0, :], rt[:, 2:3], con("first_e"), le[:, 2, :], oh[:, 0, :])
                back.then(V.scalar_tensor_tensor(out=le[:, 1, :], in0=oh[:, 0, :], scalar=-BIG, in1=le[:, 0, :], op0=ALU.mult, op1=ALU.add))
                first_of(back, le[:, 1, :], rt[:, 3:4], con("first_e"), le[:, 3, :], oh[:, 1, :])
                V.tensor_tensor(rt[:, 7:8], rt[:, 3:4], rt[:, 2:3], ALU.subtract).then_inc(s["logits_ready"], 1)
                for k in range(PICKS):
                    back(V.tensor_tensor(M[:, k, :, :], oG[:, :].unsqueeze(2).to_broadcast([P, GROUPS, PER_GROUP]),
                                         oh[:, k, :].unsqueeze(1).to_broadcast([P, GROUPS, PER_GROUP]), ALU.mult))
                back.settle()
                if not first:
                    dve.wait_ge(s["pe_rank"], j)
                Mk = M[:, :, :, :].rearrange("p k g e -> p k (g e)")
                V.tensor_tensor(M_bf[:, :], Mk[:, 0, :], Mk[:, 1, :], ALU.add).then_inc(s["routes_ready"], 1)

            def back_weights(j):
                dve.wait_ge(s["rexp_ready"], 2 * j + 2)
                back.then(V.tensor_scalar(rt[:, 4:5], rt[:, 9:10], 1.0, rt[:, 8:9], ALU.add, ALU.mult))
                back.then(V.reciprocal(rt[:, 5:6], rt[:, 4:5]))
                gates = gate_all[:, bass.ds(j, 1), :].rearrange("p a k -> p (a k)")
                back(V.tensor_copy(gates[:, 0:1], rt[:, 5:6]))
                back(V.tensor_tensor(gates[:, 1:2], rt[:, 5:6], rt[:, 9:10], ALU.mult))

            def back_rank(j, first=False):
                dve.wait_ge(s["pe_rank"], j + 1)
                back.then(V.tensor_tensor(R[:, :], bank[7][:, 64:64 + NE], counts[:, :], ALU.add))
                back(V.tensor_tensor(counts[:, :], bank[7][:, 128:128 + NE], counts[:, :], ALU.add))
                Mk = M[:, :, :, :].rearrange("p k g e -> p k (g e)")
                back(V.tensor_tensor(prod[:, :, :], Mk, R[:, :].unsqueeze(1).to_broadcast([P, PICKS, NE]), ALU.mult))
                back.then(V.tensor_tensor(prod_e[:, :, :], Mk, con("iota_e").unsqueeze(1).to_broadcast([P, PICKS, NE]), ALU.mult))
                back.then(V.tensor_reduce(rk[:, :], prod[:, :, :], AX.X, ALU.add))
                back(V.tensor_copy(rank_all[:, bass.ds(j, 1), :].rearrange("p a k -> p (a k)"), rk[:, :]))
                back(V.tensor_reduce(e_all[:, bass.ds(j, 1), :].rearrange("p a k -> p (a k)"), prod_e[:, :, :], AX.X, ALU.add))
                if not first:
                    dve.wait_ge(s["pe_idx"], j)
                for k in range(PICKS):
                    back(V.tensor_scalar(at_rank[:, k, :], con("iota_block"), rk[:, k:k + 1], None, ALU.is_equal))
                V.tensor_scalar(M_tok[:, :, :], Mk, token[:, 0:1], None, ALU.mult).then_inc(s["onehot_ready"], 1)
                back(V.tensor_scalar(token[:, :], token[:, :], float(P), None, ALU.add))

            def back_idx(j):
                dve.wait_ge(s["pe_idx"], j + 1)
                V.tensor_tensor(idx_f[:, :], idx_f[:, :], bank[7][0:BLOCK, 192:192 + NE], ALU.add).then_inc(s["idx_added"], 1)

            def body(i, first=False, last=False, second=False):
                front.begin(i)
                if not first:
                    back.begin(i - 1)
                    back_o(i - 1)
                front_gates(i, first)
                if not first:
                    back_h(i - 1)
                else:
                    dve.wait_ge(s["pe_hist_T"], 1)
                    V.tensor_copy(u_ext[:, :, 0:HIST], bank[7][:, 0:NG * HIST].rearrange("p (g n) -> p g n", g=NG)).then_inc(s["history_in"], 1)
                    dve.wait_ge(s["small_in"], 16 * (SMALL - FIRST_SMALL))
                    dve.wait_ge(s["history_in"], 1)
                front_pool(i, first)
                if not first:
                    back_turned(i - 1, second)
                front_silu(i)
                if not first:
                    back_route(i - 1, second)
                    back_rank(i - 1, second)
                front_gla(i, first)
                if not last:
                    x_turned(i + 1)
                front_state(i, first)
                if not first:
                    back_idx(i - 1)
                    back_weights(i - 1)

            dve.wait_ge(s["first_small_in"], 16 * FIRST_SMALL)
            x_turned(0, True)
            body(0, first=True)
            front.per = front.n
            body(1, second=True)
            assert front.n == front.per
            back.per = back.n
            with dve.Fori(2, TILES - 1) as i:
                body(i)
                assert (front.n, back.n) == (front.per, back.per)
            body(TILES - 1, last=True)
            V.tensor_copy(u_keep[:, 1, :, :], u_ext[:, :, P:P + HIST]).then_inc(s["u_kept"], 1)
            j = TILES - 1
            back.begin(j)
            back_o(j)
            back_h(j)
            dve.wait_ge(s["pe_small_T"], 1)
            for n in range(2):
                V.tensor_copy(pool_out[n], bank[2 + n][0:HIST, :]).then_inc(s["pool_out_ready"], 1)
            back_turned(j)
            back_route(j)
            back_rank(j)
            dve.wait_ge(s["idx_added"], TILES)
            dve.wait_ge(s["pe_idx"], TILES)
            V.tensor_tensor(idx_i[:, :], idx_f[:, :], bank[7][0:BLOCK, 192:192 + NE], ALU.add).then_inc(s["idx_ready"], 1)
            back_weights(j)

            moe = Steps(dve, s["dve_moe"])

            def rows_turned(e, b):
                for half in range(2):
                    dve.wait_ge(s["pe_eT"], e + 1)
                    k = slice(half * KD // 2, (half + 1) * KD // 2)
                    V.tensor_tensor(rowsT[b][:, k, :], bank[half][:, 0:4 * BLOCK].rearrange("p (k n) -> p k n", n=BLOCK),
                                    g_ffn[:, k].unsqueeze(2).to_broadcast([P, KD // 2, BLOCK]), ALU.mult).then_inc(s["eT_ready"], 1)

            def expert(t, b, last=False):
                e = 2 * t + b
                moe.begin(e)
                dve.wait_ge(s["sig_ready"], e + 1)
                moe.then(V.tensor_scalar(gs[:, 0:NH], sig[:, 0:NH], 1.0, None, ALU.add))
                moe.then(V.reciprocal(gs[:, 0:NH], gs[:, 0:NH]))
                moe.then(V.tensor_tensor(gs[:, 0:NH], bank[2 + b][:, 0:NH], gs[:, 0:NH], ALU.mult))
                for half in range(2):
                    dve.wait_ge(s["pe_u2"], 2 * e + half + 1)
                    part = slice(half * NH // 2, (half + 1) * NH // 2)
                    V.tensor_tensor(hid[b][:, part], bank[4 + half][:, 0:NH // 2], gs[:, part], ALU.mult).then_inc(s["hid_ready"], 1)
                moe.end()
                if not last:
                    rows_turned(e + 1, 1 - b)

            rows_turned(0, 0)
            expert(0, 0)

            expert(0, 1)

            def slots():
                st = once.then
                st(V.tensor_tensor(over[:, :, :], counts[:, :].unsqueeze(2).to_broadcast([P, NE, EXTRA_PER_E]),
                                   con("block_edge").unsqueeze(1).to_broadcast([P, NE, EXTRA_PER_E]), ALU.is_gt))
                st(V.tensor_reduce(n_extra[:, :], over[:, :, :], AX.X, ALU.add))
                st(V.tensor_tensor_scan(upto[:, :], ones_bf[:, 0:NE], n_extra[:, :], 0.0, ALU.mult, ALU.add))
                st(V.tensor_tensor(base_e[:, :], upto[:, :], n_extra[:, :], ALU.subtract))
                e_flat = e_all[:, :, :].rearrange("p t k -> p (t k)")
                r_flat = rank_all[:, :, :].rearrange("p t k -> p (t k)")
                st(V.tensor_tensor(is_e[:, :, :], e_flat.unsqueeze(2).to_broadcast([P, NP, NE]),
                                   con("iota_e").unsqueeze(1).to_broadcast([P, NP, NE]), ALU.is_equal))
                st(V.tensor_tensor(is_e[:, :, :], is_e[:, :, :], base_e[:, :].unsqueeze(1).to_broadcast([P, NP, NE]), ALU.mult))
                st(V.tensor_reduce(slot_t[:, 0, :], is_e[:, :, :], AX.X, ALU.add))
                st(V.scalar_tensor_tensor(out=slot_f[:, :], in0=e_flat, scalar=float(BLOCK), in1=r_flat, op0=ALU.mult, op1=ALU.add))
                st(V.tensor_scalar(slot_t[:, 0, :], slot_t[:, 0, :], float(NE - 1), None, ALU.add))
                st(V.tensor_tensor(slot_t[:, 0, :], slot_t[:, 0, :], e_flat, ALU.subtract))
                st(V.tensor_scalar(slot_t[:, 1, :], r_flat, float(BLOCK), float(BLOCK), ALU.is_ge, ALU.mult))
                st(V.tensor_tensor(slot_t[:, 0, :], slot_t[:, 0, :], slot_t[:, 1, :], ALU.mult))
                st(V.tensor_tensor(slot_f[:, :], slot_f[:, :], slot_t[:, 0, :], ALU.add))
                st(V.tensor_copy(slot_i[:, :], slot_f[:, :]))
                st(V.tensor_tensor(own_x[:, :, :], con("iota_x").unsqueeze(2).to_broadcast([P, EXTRA, NE]),
                                   upto[:, :].unsqueeze(1).to_broadcast([P, EXTRA, NE]), ALU.is_ge))
                st(V.tensor_reduce(x_of[:, :], own_x[:, :, :], AX.X, ALU.add))
                st(V.tensor_copy(steer[0:1, 0:1], upto[0:1, NE - 1:NE]))
                st(V.tensor_scalar(x_of[:, :], x_of[:, :], float(NE - 1), None, ALU.min))
                V.tensor_copy(steer[0:1, 1:], x_of[0:1, :]).then_inc(s["slots_ready"], 1)

            slots()
            with dve.Fori(1, NE // 2 - 1) as t:
                expert(t, 0)
                expert(t, 1)
            expert(NE // 2 - 1, 0)
            expert(NE // 2 - 1, 1, last=True)

            dve.wait_ge(s["slots_ready"], 1)
            n_x = dve.value_load(steer[0:1, 0:1], min_val=0, max_val=EXTRA)
            xt = Steps(dve, s["x_tab_dve"])
            once.then(V.tensor_copy(token[:, :], con("token")))
            once.then(V.memset(idx_xf[:, :], 0.0))

            def table(n):
                xt.begin(n)
                st = xt.then
                st(V.tensor_scalar(x_at[:, 0:1], slot_f[:, bass.ds(n, 1)], float(-NE * BLOCK), None, ALU.add))
                st(V.tensor_scalar(x_lo[:, :], con("edge_x"), x_at[:, 0:1], None, ALU.is_le))
                st(V.tensor_scalar(x_hi[:, :], con("edge_x"), float(BLOCK), x_at[:, 0:1], ALU.add, ALU.is_gt))
                st(V.tensor_tensor(x_lo[:, :], x_lo[:, :], x_hi[:, :], ALU.mult))
                st(V.tensor_tensor(x_hi[:, :], x_lo[:, :], con("edge_x"), ALU.mult))
                st(V.tensor_reduce(x_at[:, 1:2], x_hi[:, :], AX.X, ALU.add))
                st(V.tensor_tensor(x_at[:, 2:3], x_at[:, 0:1], x_at[:, 1:2], ALU.subtract))
                st(V.tensor_scalar(at_rank[:, 0, :], con("iota_block"), x_at[:, 2:3], None, ALU.is_equal))
                st(V.tensor_scalar(x_hi[:, :], x_lo[:, :], token[:, 0:1], None, ALU.mult))
                dve.wait_ge(s["x_tab_pe"], n + 1)
                st(V.tensor_tensor(idx_xf[:, :], idx_xf[:, :], bank[7][0:BLOCK, 0:EXTRA], ALU.add))
                xt.end()

            with dve.If(n_x > 0):
                xt.per = TABLE_STEPS
                with dve.Fori(0, TILES) as i:
                    table(2 * i)
                    table(2 * i + 1)
                    V.tensor_scalar(token[:, :], token[:, :], float(P), None, ALU.add).then_inc(s["x_dve"], 1)
                    dve.wait_ge(s["x_dve"], i + 1)
                V.tensor_copy(idx_xi[:, :], idx_xf[:, :]).then_inc(s["x_idx_ready"], 1)
            with dve.Else():
                V.memset(idx_xi[:, :], 0).then_inc(s["x_idx_ready"], 1)
            with dve.If(n_x > 0):
                with dve.Fori(0, EXTRA) as n:
                    with dve.If(n < n_x):
                        c = X_STEPS * n + TILES
                        st = [0]

                        def step(ins):
                            ins.then_inc(s["x_dve"], 1)
                            st[0] += 1
                            wait_parted(dve, s["x_dve"], c + st[0], s["parted"])
                        dve.wait_ge(s["x_pe"], 4 * n + 1)
                        for half in range(2):
                            k = slice(half * KD // 2, (half + 1) * KD // 2)
                            step(V.tensor_tensor(rowsT[0][:, k, :], bank[half][:, 0:4 * BLOCK].rearrange("p (k n) -> p k n", n=BLOCK),
                                                 g_ffn[:, k].unsqueeze(2).to_broadcast([P, KD // 2, BLOCK]), ALU.mult))
                        dve.wait_ge(s["x_act"], 3 * n + 1)
                        step(V.tensor_scalar(gs[:, 0:NH], sig[:, 0:NH], 1.0, None, ALU.add))
                        step(V.reciprocal(gs[:, 0:NH], gs[:, 0:NH]))
                        step(V.tensor_tensor(gs[:, 0:NH], bank[2][:, 0:NH], gs[:, 0:NH], ALU.mult))
                        dve.wait_ge(s["x_pe"], 4 * n + 3)
                        step(V.tensor_tensor(hid[0][:, 0:NH], bank[4][:, 0:NH], gs[:, 0:NH], ALU.mult))

            final = Steps(dve, s["dve_fin"])

            def combine(i):
                dve.wait_ge(y_in[i], 32)
                final.then(V.scalar_tensor_tensor(out=y1[i], in0=y1[i], scalar=gate_all[:, i, 0:1], in1=h_all[:, i, :], op0=ALU.mult, op1=ALU.add))
                V.scalar_tensor_tensor(out=y1[i], in0=y2[i], scalar=gate_all[:, i, 1:2], in1=y1[i], op0=ALU.mult, op1=ALU.add).then_inc(s["fin_ready"], 1)

            def normalize(i):
                dve.wait_ge(s["frstd_ready"], i + 1)
                V.scalar_tensor_tensor(out=y2[i], in0=y1[i], scalar=fss[:, i:i + 1], in1=g_fin, op0=ALU.mult, op1=ALU.mult).then_inc(s["out_ready"], 1)

            dve.wait_ge(s["g_fin_in"], 16)
            for i in range(TILES):
                combine(i)
                if i:
                    normalize(i - 1)
            normalize(TILES - 1)

        @block.tensor
        def _(pe):
            mm = nc.tensor.matmul

            def turn(out, src, n):
                return nc.tensor.transpose(out, src, ident[0:n, 0:n])

            def turn_x(i):
                pe.wait_ge(s["xs_ready"], i + 1)
                for half in range(2):
                    for k in range(4):
                        last = turn(bank[half][:, k * P:(k + 1) * P], xs[:, 4 * half + k, :], P)
                    last.then_inc(s["pe_xT"], 1)

            def features(out, a, b):
                for k in range(KD):
                    last = mm(out, w_in_sb[:, k, a:b], xnT[:, k, :], start=k == 0, stop=k == KD - 1)
                return last

            def proj_z(i, first=False):
                if first:
                    pe.wait_ge(s["w_z_in"], 16)
                pe.wait_ge(s["xnT_ready"], 2 * i + 2)
                features(bank[3][0:RANK, 0:P], Z0, D_IN).then_inc(s["pe_z"], 1)

            def proj_qk_gate(i, first=False):
                if first:
                    pe.wait_ge(s["w_qk_in"], 16)
                for m in range(2 * PAIRS):
                    last = features(bank[2][:, m * P:(m + 1) * P], Q0 + m * P, Q0 + (m + 1) * P)
                    if m == 0:
                        if first:
                            pe.wait_ge(s["first_small_in"], 16 * FIRST_SMALL)
                        pe.wait_ge(s["z_ready"], i + 1)
                        for g in range(PAIRS):
                            gate = mm(bank[3][:, (1 + g) * P:(2 + g) * P], w_up_sb[:, g * P:(g + 1) * P], z_sb[:, :], start=True, stop=True)
                        gate.then_inc(s["pe_gate"], 1)
                last.then_inc(s["pe_qk"], 1)

            def proj_u(i, first=False):
                if first:
                    pe.wait_ge(s["w_u_in"], 16)
                else:
                    pe.wait_ge(s["mixo_ready"], i)
                for m in range(NG):
                    last = features(bank[4][:, m * P:(m + 1) * P], U0 + m * P, U0 + (m + 1) * P)
                last.then_inc(s["pe_u"], 1)

            def proj_r(i, first=False):
                if first:
                    pe.wait_ge(s["w_r_in"], 16)
                for m in range(HEADS):
                    last = features(bank[5][:, m * P:(m + 1) * P], R0 + m * P, R0 + (m + 1) * P)
                last.then_inc(s["pe_r"], 1)

            def proj_v(i, part, first=False):
                if first:
                    pe.wait_ge(s["w_v_in"], 16)
                elif part == 0:
                    pe.wait_ge(s["sA_ready"], i)
                for k in range(part * KD // 2, (part + 1) * KD // 2):
                    last = mm(bank[6][:, :], xnT[:, k, :], w_in_sb[:, k, V0:R0], start=k == 0, stop=k == KD - 1)
                if part:
                    last.then_inc(s["pe_v"], 1)

            def pool_mix(i):
                pe.wait_ge(s["pooled_ready"], i + 1)
                for g in range(NG):
                    last = mm(bank[4][:, g * P:(g + 1) * P], w_pool_sb[:, g, :], pooled[:, g, :], start=True, stop=True)
                last.then_inc(s["pe_pool"], 1)

            def turn_k(i):
                pe.wait_ge(s["kdec_ready"], i + 1)
                for p in range(PAIRS):
                    last = turn(bank[2][:, p * P:(p + 1) * P], k_dec[:, p, :], P)
                last.then_inc(s["pe_kT"], 1)

            def gla(i, first=False):
                pe.wait_ge(s["qi_ready"], 2 * i + 2)
                pe.wait_ge(s["ki_ready"], i + 1)
                pe.wait_ge(s["silu_ready"], i + 1)
                for h in range(HEADS):
                    last = mm(bank[5][:, h * P:(h + 1) * P], k_i[:, h // 2, :], q_i[:, h, :], start=True, stop=True)
                last.then_inc(s["pe_scores"], 1)
                pe.wait_ge(s["v_ready"], i + 1)
                pe.wait_ge(s["kz_ready"], 2 * i + 2)
                for c, out, signal in ((0, bank[3], s["pe_kvA"]), (1, bank[6], s["pe_kvB"])):
                    for p in range(PAIRS):
                        last = mm(out[:, 2 * p * DV:(2 * p + 2) * DV], kz[:, c, p, :], v_sb[:, 2 * p * DV:(2 * p + 2) * DV],
                                  start=True, stop=True)
                    last.then_inc(signal, 1)
                pe.wait_ge(s["sc_ready"], i + 1)
                pe.wait_ge(s["mixp_ready"], i + 1)
                o_bank = bank[4][:, :].rearrange("p (h n) -> p h n", h=HEADS)
                for h in range(HEADS):
                    mm(o_bank[:, h, :], v_sb[:, h * DV:(h + 1) * DV], sc[:, h, :], start=h == 0, stop=False)
                if first:
                    pe.wait_ge(s["setup_pool"], 4)
                    pe.wait_ge(s["s_sample_ready"], 1)
                else:
                    pe.wait_ge(s["sB_ready"], i)
                    pe.wait_ge(s["sA_ready"], i)
                for p in range(PAIRS):
                    for c, state in ((0, sA), (1, sB)):
                        cols = slice(c * CHUNK, (c + 1) * CHUNK)
                        last = mm(o_bank[:, 2 * p:2 * p + 2, cols], state[:, p, :], q_i[:, 2 * p:2 * p + 2, cols],
                                  start=False, stop=p == PAIRS - 1 and c == 1)
                last.then_inc(s["pe_o"], 1)

            def head_means(j):
                pe.wait_ge(s["osq_ready"], j + 1)
                mm(bank[5][:, :], one_dv[:, :], osq[:, :, :].rearrange("p h n -> p (h n)"), start=True, stop=True).then_inc(s["pe_ones"], 1)

            def project_out(j, first=False):
                pe.wait_ge(s["mixo_ready"], j + 1)
                pe.wait_ge(s["w_out_scaled"], KD)
                for half in range(2):
                    for k in range(KD):
                        last = mm(bank[half][:, :], mixT[:, k, :], w_out_sb[:, k, half * 512:(half + 1) * 512], start=k == 0, stop=k == KD - 1)
                last.then_inc(s["pe_wout"], 1)

            def turn_h(j):
                pe.wait_ge(s["hs_ready"], j + 1)
                for half in range(2):
                    for k in range(4):
                        last = turn(bank[half][:, k * P:(k + 1) * P], hs[:, 4 * half + k, :], P)
                    last.then_inc(s["pe_hT"], 1)

            def router(j):
                pe.wait_ge(s["hnT_ready"], 2 * j + 2)
                pe.wait_ge(s["idx_added"], j + 1)
                for k in range(KD):
                    last = mm(bank[7][:, 0:NL], hnT[:, k, :], w_r_sb[:, k, :], start=k == 0, stop=k == KD - 1)
                last.then_inc(s["pe_router"], 1)

            def ranks(j):
                pe.wait_ge(s["routes_ready"], j + 1)
                mm(bank[7][:, 64:64 + NE], before_bf[:, :], M_bf[:, :], start=True, stop=True)
                mm(bank[7][:, 128:128 + NE], ones_bf[:, :], M_bf[:, :], start=True, stop=True).then_inc(s["pe_rank"], 1)

            def mark(j):
                pe.wait_ge(s["onehot_ready"], j + 1)
                for k in range(PICKS):
                    last = mm(bank[7][0:BLOCK, 192:192 + NE], at_rank[:, k, :], M_tok[:, k, :], start=k == 0, stop=k == PICKS - 1)
                last.then_inc(s["pe_idx"], 1)

            def turn_history():
                for g in range(NG):
                    last = turn(bank[7][:, g * HIST:(g + 1) * HIST], pool_in[:, g * P:(g + 1) * P], HIST)
                last.then_inc(s["pe_hist_T"], 1)

            def body(i, first=False, last=False):
                proj_z(i, first)
                if not first:
                    head_means(i - 1)
                proj_qk_gate(i, first)
                proj_u(i, first)
                if first:
                    pe.wait_ge(s["small_in"], 16 * (SMALL - FIRST_SMALL))
                    turn_history()
                if not first:
                    project_out(i - 1)
                proj_r(i, first)
                if not first:
                    turn_h(i - 1)
                proj_v(i, 0, first)
                if not first:
                    router(i - 1)
                proj_v(i, 1)
                pool_mix(i)
                if not first:
                    ranks(i - 1)
                if not last:
                    turn_x(i + 1)
                turn_k(i)
                gla(i, first)
                if not first:
                    mark(i - 1)

            pe.wait_ge(s["consts_in"], 16)
            turn_x(0)
            pe.wait_ge(s["setup_dve"], 7)
            body(0, first=True)
            with pe.Fori(1, TILES - 1) as i:
                body(i)
            body(TILES - 1, last=True)
            j = TILES - 1
            head_means(j)
            project_out(j)
            pe.wait_ge(s["u_kept"], 2)
            for n in range(2):
                for g in range(NG):
                    last = turn(bank[2 + n][0:HIST, g * P:(g + 1) * P], u_keep[:, n, g, :], P)
            last.then_inc(s["pe_small_T"], 1)
            turn_h(j)
            router(j)
            ranks(j)
            mark(j)

            HALVES = (range(0, KF // 2), range(KF // 2, KF))

            def turn_rows(e, b, count):
                pe.wait_ge(rows_in[b], count)
                for half in range(2):
                    for k in range(4):
                        c = (4 * half + k) * P
                        last = turn(bank[half][:, k * BLOCK:(k + 1) * BLOCK], rows[b][:, c:c + P], BLOCK)
                last.then_inc(s["pe_eT"], 1)

            def up(out, w, b, blocks=range(KF)):
                for n, m in enumerate(blocks):
                    for k in range(KD):
                        last = mm(out[:, n * BLOCK:(n + 1) * BLOCK], w[:, k, m * P:(m + 1) * P], rowsT[b][:, k, :], start=k == 0, stop=k == KD - 1)
                return last

            def expert(t, b, last=False):
                e = 2 * t + b
                pe.wait_ge(s["eT_ready"], 2 * e + 2)
                pe.wait_ge(g_in[b], 16 * t + 16)
                up(bank[2 + b], wg[b], b).then_inc(s["pe_g"], 1)
                pe.wait_ge(u_in[b], 16 * t + 16)
                for half in range(2):
                    up(bank[4 + half], wu[b], b, HALVES[half]).then_inc(s["pe_u2"], 1)
                if not last:
                    turn_rows(e + 1, 1 - b, 16 * (t + b) + 16)
                pe.wait_ge(d_in[b], 16 * t + 16)
                pe.wait_ge(s["hid_ready"], 2 * e + 2)
                if not (isinstance(t, int) and e == 0):
                    pe.wait_ge(s["ye_ready"], 2 * e)
                for half in range(2):
                    for k in range(KF):
                        ins = mm(bank[6 + half][0:BLOCK, :], hid[b][:, k * BLOCK:(k + 1) * BLOCK], wd[b][:, k, half * 512:(half + 1) * 512],
                                 start=k == 0, stop=k == KF - 1)
                    ins.then_inc(s["pe_d"] if half else s["pe_d0"], 1)

            turn_rows(0, 0, 16)
            pe.wait_ge(s["pool_out_ready"], 2)
            expert(0, 0)
            expert(0, 1)
            with pe.Fori(1, NE // 2 - 1) as t:
                expert(t, 0)
                expert(t, 1)
            expert(NE // 2 - 1, 0)
            expert(NE // 2 - 1, 1, last=True)

            pe.wait_ge(s["slots_ready"], 1)
            n_x = pe.value_load(steer[0:1, 0:1], min_val=0, max_val=EXTRA)
            pe.wait_ge(s["ye_ready"], 2 * NE)
            with pe.If(n_x > 0):
                with pe.Fori(0, NP) as n:
                    pe.wait_ge(s["x_tab_dve"], TABLE_STEPS * n + TABLE_STEPS - 1)
                    mm(bank[7][0:BLOCK, 0:EXTRA], at_rank[:, 0, :], x_hi[:, :], start=True, stop=True).then_inc(s["x_tab_pe"], 1)
                pe.nop()
            with pe.If(n_x > 0):
                with pe.Fori(0, EXTRA) as n:
                    with pe.If(n < n_x):
                        pe.wait_ge(s["x_rows"], 16 * n + 16)
                        for half in range(2):
                            for k in range(4):
                                c = (4 * half + k) * P
                                last = turn(bank[half][:, k * BLOCK:(k + 1) * BLOCK], rows[0][:, c:c + P], BLOCK)
                        last.then_inc(s["x_pe"], 1)
                        pe.wait_ge(s["x_w"], 48 * n + 48)
                        pe.wait_ge(s["x_dve"], X_STEPS * n + TILES + 2)
                        up(bank[2], wg[0], 0).then_inc(s["x_pe"], 1)
                        up(bank[4], wu[0], 0).then_inc(s["x_pe"], 1)
                        pe.wait_ge(s["x_dve"], X_STEPS * n + TILES + X_STEPS)
                        for half in range(2):
                            for k in range(KF):
                                last = mm(bank[6 + half][0:BLOCK, :], hid[0][:, k * BLOCK:(k + 1) * BLOCK], wd[0][:, k, half * 512:(half + 1) * 512],
                                          start=k == 0, stop=k == KF - 1)
                        last.then_inc(s["x_pe"], 1)


def kernel(**inputs):
    import concourse.bacc as bacc
    from concourse.bass_utils import run_bass_kernel_spmd

    nc = bacc.Bacc("TRN2", target_bir_lowering=False, num_devices=1)
    a = {k: np.asarray(v) for k, v in inputs.items()}
    pads = np.zeros((PADS, D), np.float32)
    data = {
        "x_all": np.concatenate([a["x_sample"][0], pads, a["meta_tokens"], a["x_prompt"][0]], axis=0),
        "state_pool": a["state_pool"][0, 0],
        "state_gla": a["state_gla"][0, 0],
        "norm_mix": a["norm_mix"][0],
        "w_in": a["w_in"][0],
        "w_gate_up": a["w_gate_up"][0],
        "b_gate": a["b_gate"][0],
        "w_pool": a["w_pool"][0],
        "pool_scale": a["pool_scale"][0],
        "gla_norm": a["gla_norm"][0],
        "w_out": a["w_out"][0],
        "norm_ffn": a["norm_ffn"][0],
        "w_router": np.concatenate([a["w_router_group"][0], a["w_router_expert"][0]], axis=1),
        "b_router": np.concatenate([a["b_router_group"][0], a["b_router_expert"][0]], axis=0),
        "w_eg": a["w_expert_gate"][0].reshape(NE * D, FF),
        "w_eu": a["w_expert_up"][0].reshape(NE * D, FF),
        "w_ed": a["w_expert_down"][0].reshape(NE * FF, D),
        "norm_final": a["norm_final"],
        "const": constants(),
    }
    arrays, args = {}, []
    for name, v in data.items():
        v = np.ascontiguousarray(v)
        arrays[f"in_{name}"] = v
        args.append(nc.dram_tensor(f"in_{name}", v.shape, F32, kind="ExternalInput").ap())
    outs = [("y_prompt", (SEQ, D), (1, SEQ, D)), ("y_sample", (SAMPLE, D), (1, SAMPLE, D)),
            ("pool_prompt", (HIST, D_POOL), (1, 1, HIST, D_POOL)), ("gla_prompt", (HEADS, DK, DV), (1, 1, HEADS, DK, DV)),
            ("pool_sample", (HIST, D_POOL), (1, 1, HIST, D_POOL)), ("gla_sample", (HEADS, DK, DV), (1, 1, HEADS, DK, DV))]
    for name, shape, _ in outs:
        args.append(nc.dram_tensor(f"out_{name}", shape, F32, kind="ExternalOutput").ap())
    build(nc, *args)
    r = run_bass_kernel_spmd(nc, [arrays], core_ids=[0])
    return tuple(r.results[0][f"out_{name}"].reshape(shape) for name, _, shape in outs)
```
